# Optimizing a Trainium2 kernel written in Bass

```python
import jax, jax.numpy as jnp
from jax import lax
import numpy as np

D_MODEL = 1024
BATCH = 1
SEQ = 2048
DEPTH = 1

N_MIXERS = 4
EPS = 1e-6
D_FF = 4 * D_MODEL

A_CHUNK = 128
A_GROUPS = 8
A_WIDTH = D_MODEL
A_GDIM = A_WIDTH // A_GROUPS

B_WIDTH = D_MODEL
B_KSIZE = 3

C_WINDOWS = (2, 4, 8, 16)
C_GROUPS = len(C_WINDOWS)
C_GDIM = D_MODEL // C_GROUPS

D_HEADS = 16
D_LAT = 128
D_VDIM = D_MODEL // D_HEADS
D_IDX_HEADS = 8
D_IDX_DIM = 64
D_TOPK_MAX = 256
D_QBLOCK = 128
D_SPLITS = (D_HEADS * D_LAT,
            D_HEADS * D_LAT + D_LAT,
            D_HEADS * D_LAT + D_LAT + D_IDX_HEADS * D_IDX_DIM,
            D_HEADS * D_LAT + D_LAT + D_IDX_HEADS * D_IDX_DIM + D_IDX_DIM)
D_IN_COLS = D_SPLITS[-1] + D_IDX_HEADS

kernel_name = "hybrid_interleaved_sgu_conv_pool_dsa"

def _type_counts():
    return [sum(1 for i in range(DEPTH) if i % N_MIXERS == m) for m in range(N_MIXERS)]

def rmsnorm(x, g):
    xf = x.astype(jnp.float32)
    y = xf * lax.rsqrt(jnp.mean(xf * xf, axis=-1, keepdims=True) + EPS)
    return (y * g.astype(jnp.float32)).astype(x.dtype)

def mixer_chunked_sgu(h, w_in, v_g, w_s, b_s, w_out):
    bsz, L, _ = h.shape
    z = jax.nn.gelu(h @ w_in)
    u, v = jnp.split(z, 2, axis=-1)
    v = rmsnorm(v, v_g)
    n = L // A_CHUNK
    v = v.reshape(bsz, n, A_CHUNK, A_GROUPS, A_GDIM)
    causal = jnp.tril(jnp.ones((A_CHUNK, A_CHUNK), dtype=bool))
    ws = jnp.where(causal[None], w_s, jnp.zeros_like(w_s)).astype(v.dtype)
    s = jnp.einsum('gts,bnsgc->bntgc', ws, v) + b_s.T.astype(v.dtype)[None, None, :, :, None]
    s = s.reshape(bsz, L, A_WIDTH)
    return (u * s) @ w_out

def mixer_short_conv(h, w_in, conv_w, w_out):
    bg, cg, hv = jnp.split(h @ w_in, 3, axis=-1)
    z = cg * hv
    y = lax.conv_general_dilated(z, conv_w.astype(z.dtype), window_strides=(1,),
                                 padding=[(B_KSIZE - 1, 0)],
                                 dimension_numbers=('NWC', 'WIO', 'NWC'),
                                 feature_group_count=B_WIDTH)
    return (bg * y) @ w_out

def mixer_multiscale_pool(h, w_in, w_grp, scale):
    bsz, L, _ = h.shape
    z = h @ w_in
    zf = z.astype(jnp.float32).reshape(bsz, L, C_GROUPS, C_GDIM)
    cs = jnp.cumsum(zf, axis=1)
    cs = jnp.concatenate([jnp.zeros_like(cs[:, :1]), cs], axis=1)
    t = jnp.arange(L)
    pooled = []
    for g, w in enumerate(C_WINDOWS):
        lo = jnp.maximum(t + 1 - w, 0)
        seg = cs[:, 1:, g] - cs[:, lo, g]
        cnt = (t + 1 - lo).astype(jnp.float32)
        pooled.append(seg / cnt[None, :, None])
    pooled = jnp.stack(pooled, axis=2) - zf
    y = jnp.einsum('blgc,gcd->blgd', pooled.astype(z.dtype), w_grp)
    return y.reshape(bsz, L, D_MODEL) * scale

def mixer_dsa(h, w_in, kv_g, w_uv, w_out):
    bsz, L, _ = h.shape
    topk = min(D_TOPK_MAX, L // 4)
    q, c, qi, ki, wi = jnp.split(h @ w_in, list(D_SPLITS), axis=-1)
    q = q.reshape(bsz, L, D_HEADS, D_LAT)
    c = rmsnorm(c, kv_g)
    qi = qi.reshape(bsz, L, D_IDX_HEADS, D_IDX_DIM)
    wi = wi * (D_IDX_HEADS ** -0.5 * D_IDX_DIM ** -0.5)
    n_blk = L // D_QBLOCK
    key_pos = jnp.arange(L)

    def to_blocks(a):
        return a.reshape(bsz, n_blk, D_QBLOCK, *a.shape[2:]).swapaxes(0, 1)

    def block(args):
        qb, qib, wib, blk = args
        qpos = blk * D_QBLOCK + jnp.arange(D_QBLOCK)
        logits = jnp.einsum('bthd,bsd->bths', qib, ki)
        score = jnp.einsum('bths,bth->bts', jax.nn.relu(logits).astype(jnp.float32),
                           wib.astype(jnp.float32))
        causal = key_pos[None, :] <= qpos[:, None]
        score = jnp.where(causal[None], score, -jnp.inf)
        _, idx = lax.top_k(score, topk)
        kv_sel = jax.vmap(lambda cb, ib: cb[ib])(c, idx)
        valid = idx <= qpos[None, :, None]
        att = jnp.einsum('bthd,btkd->bthk', qb, kv_sel).astype(jnp.float32) * (D_LAT ** -0.5)
        att = jnp.where(valid[:, :, None, :], att, -jnp.inf)
        p = jax.nn.softmax(att, axis=-1).astype(c.dtype)
        return jnp.einsum('bthk,btkd->bthd', p, kv_sel)

    o = lax.map(block, (to_blocks(q), to_blocks(qi), to_blocks(wi), jnp.arange(n_blk)))
    o = o.swapaxes(0, 1).reshape(bsz, L, D_HEADS, D_LAT)
    o = jnp.einsum('blhc,hcv->blhv', o, w_uv).reshape(bsz, L, D_HEADS * D_VDIM)
    return o @ w_out

def channel_mlp(h, w1, w2):
    a = jax.nn.relu(h @ w1)
    return (a * a) @ w2

def setup_inputs(seed: int = 0) -> dict:
    key = jax.random.key(seed)
    ks = iter(jax.random.split(key, 32))
    nA, nB, nC, nD = _type_counts()
    f32 = jnp.float32

    def nrm(shape, scale):
        return jax.random.normal(next(ks), shape, f32) * scale

    def gain(shape):
        return 1.0 + 0.02 * jax.random.normal(next(ks), shape, f32)

    return {
        "x": jax.random.normal(next(ks), (BATCH, SEQ, D_MODEL), f32),
        "norm_mix_g": gain((DEPTH, D_MODEL)),
        "norm_mlp_g": gain((DEPTH, D_MODEL)),
        "final_g": gain((D_MODEL,)),
        "a_w_in": nrm((nA, D_MODEL, 2 * A_WIDTH), D_MODEL ** -0.5),
        "a_v_g": gain((nA, A_WIDTH)),
        "a_w_s": nrm((nA, A_GROUPS, A_CHUNK, A_CHUNK), A_CHUNK ** -0.5),
        "a_b_s": gain((nA, A_GROUPS, A_CHUNK)),
        "a_w_out": nrm((nA, A_WIDTH, D_MODEL), A_WIDTH ** -0.5),
        "b_w_in": nrm((nB, D_MODEL, 3 * B_WIDTH), D_MODEL ** -0.5),
        "b_conv_w": nrm((nB, B_KSIZE, 1, B_WIDTH), B_KSIZE ** -0.5),
        "b_w_out": nrm((nB, B_WIDTH, D_MODEL), B_WIDTH ** -0.5),
        "c_w_in": nrm((nC, D_MODEL, D_MODEL), D_MODEL ** -0.5),
        "c_w_grp": nrm((nC, C_GROUPS, C_GDIM, C_GDIM), C_GDIM ** -0.5),
        "c_scale": gain((nC, D_MODEL)),
        "d_w_in": nrm((nD, D_MODEL, D_IN_COLS), D_MODEL ** -0.5),
        "d_kv_g": gain((nD, D_LAT)),
        "d_w_uv": nrm((nD, D_HEADS, D_LAT, D_VDIM), D_LAT ** -0.5),
        "d_w_out": nrm((nD, D_HEADS * D_VDIM, D_MODEL), (D_HEADS * D_VDIM) ** -0.5),
        "mlp_w1": nrm((DEPTH, D_MODEL, D_FF), D_MODEL ** -0.5),
        "mlp_w2": nrm((DEPTH, D_FF, D_MODEL), D_FF ** -0.5),
    }

def reference(x, norm_mix_g, norm_mlp_g, final_g, a_w_in, a_v_g, a_w_s, a_b_s, a_w_out,
              b_w_in, b_conv_w, b_w_out, c_w_in, c_w_grp, c_scale,
              d_w_in, d_kv_g, d_w_uv, d_w_out, mlp_w1, mlp_w2):
    for i in range(DEPTH):
        m, j = i % N_MIXERS, i // N_MIXERS
        h = rmsnorm(x, norm_mix_g[i])
        if m == 0:
            y = mixer_chunked_sgu(h, a_w_in[j], a_v_g[j], a_w_s[j], a_b_s[j], a_w_out[j])
        elif m == 1:
            y = mixer_short_conv(h, b_w_in[j], b_conv_w[j], b_w_out[j])
        elif m == 2:
            y = mixer_multiscale_pool(h, c_w_in[j], c_w_grp[j], c_scale[j])
        else:
            y = mixer_dsa(h, d_w_in[j], d_kv_g[j], d_w_uv[j], d_w_out[j])
        x = x + y
        x = x + channel_mlp(rmsnorm(x, norm_mlp_g[i]), mlp_w1[i], mlp_w2[i])
    return rmsnorm(x, final_g)


_drawn_inputs = setup_inputs


def setup_inputs(seed=0):
    import zlib

    import numpy as np

    out = dict(_drawn_inputs(seed))
    spreads = {}
    factors = {'norm_mix_g': 3.306,
     'norm_mlp_g': 12.53,
     'final_g': 9.009,
     'a_v_g': 26.976,
     'a_b_s': 18.958}
    for name, (base, spread) in spreads.items():
        noise = np.random.default_rng([zlib.crc32(name.encode()), seed]).standard_normal(out[name].shape)
        drawn = base * np.exp(spread * noise) if base else spread * noise
        out[name] = __import__('jax').numpy.asarray(drawn.astype(out[name].dtype))
    for name, factor in factors.items():
        out[name] = (out[name] * factor).astype(out[name].dtype)
    return out
```

```python
from contextlib import ExitStack

import concourse.bass as bass
from concourse import mybir

ALU = mybir.AluOpType
ACT = mybir.ActivationFunctionType
F32 = mybir.dt.float32
F32R = mybir.dt.float32r
BF16 = mybir.dt.bfloat16

P = 128
N = 512
EPS = 1e-6
SLOTS = 4
HI, LO = 0, 1
PASSES = ((HI, HI), (HI, LO), (LO, HI))
PRIMED = 8


class Turn:

    def __init__(self, i, h):
        self.i, self.h = i, h

    def __add__(self, n):
        return Turn(self.i, self.h + n)

    def __sub__(self, n):
        return Turn(self.i, self.h - n)


def slot_of(h):
    return (h.h if isinstance(h, Turn) else h) % SLOTS


def build(nc: bass.Bass, x, norm_mix_g, norm_mlp_g, final_g, a_w_in, a_v_g, a_w_s, a_b_s, a_w_out,
          mlp_w1, mlp_w2, out):
    _, L, D = x.shape
    F = mlp_w1.shape[2]
    G = a_w_s.shape[1]
    KD = D // P
    TT = N // P
    KU = 4
    BLOCKS = L // N
    GROUPS = F // N
    PAIRS = GROUPS // 2 - 1
    assert D == 2 * N and G == KD == 8 and a_w_s.shape[2] == P and KU * P == N
    assert GROUPS % 2 == 0 and L % N == 0 and BLOCKS >= 2

    UV, UU, UO, UM = 0, 4, 8, 12
    LOOP0 = UM + 2
    PER_TURN = 8
    TAIL = LOOP0 + PER_TURN * PAIRS
    UNITS = TAIL + 6
    assert UNITS % SLOTS == 0 and PER_TURN % SLOTS == 0
    M1S = GROUPS * TT
    M2S = GROUPS * 2 * TT

    x_v = x.rearrange("a (b t p) d -> (a b) p t d", t=TT, p=P)
    out_v = out.rearrange("a (b t p) d -> (a b) p t d", t=TT, p=P)
    w_in_v = a_w_in.rearrange("a (k p) f -> p (a k) f", p=P)
    w_out_v = a_w_out.rearrange("a (k p) f -> p (a k) f", p=P)
    w1_v = mlp_w1.rearrange("a (k p) (e f) -> e p (a k) f", p=P, f=N)
    w2_v = mlp_w2.rearrange("a (e k p) d -> e p (a k) d", p=P, k=KU)

    ROW = 4 * D
    PAIR_OPERAND = KD * N * 4
    at = [(nc.sbuf_base + 31) // 32 * 32]

    def region(nbytes):
        start = at[0]
        at[0] += nbytes
        return start

    def sb(name, shape, dt, offset):
        return nc.alloc_sbuf_tensor_at(name, shape, dt, offset=offset)

    A = region(2 * PAIR_OPERAND)
    B = region(2 * PAIR_OPERAND)
    C = region(2 * PAIR_OPERAND)
    hT = [sb(f"hT_{n}", [P, KD, N], F32R, A + i * PAIR_OPERAND) for i, n in enumerate(("hi", "lo"))]
    yT = [sb(f"yT_{n}", [P, KD, N], F32R, A + i * PAIR_OPERAND) for i, n in enumerate(("hi", "lo"))]
    vn = [sb(f"vn_{n}", [P, TT, D], F32R, B + i * PAIR_OPERAND) for i, n in enumerate(("hi", "lo"))]
    a2 = [[sb(f"a2_{n}{e}", [P, KU, N], F32R, B + (2 * e + i) * KU * N * 4)
           for i, n in enumerate(("hi", "lo"))] for e in range(2)]
    xin = sb("xin", [P, TT, D], F32, C)
    vf = sb("vf", [P, TT, D], F32, C)
    uT = sb("uT", [P, KD, N], F32, C + PAIR_OPERAND)
    x1T = [sb(f"x1T_{n}", [P, KD, N], F32R, C + i * PAIR_OPERAND) for i, n in enumerate(("hi", "lo"))]
    x1 = sb("x1", [P, TT, D], F32, region(TT * ROW))
    UNIT = KU * N * 4
    ring = region(2 * SLOTS * UNIT)
    w_raw = [sb(f"w_raw{s}", [P, KU, N], F32, ring + 2 * s * UNIT) for s in range(SLOTS)]
    w_lo = [sb(f"w_lo{s}", [P, KU, N], F32R, ring + 2 * s * UNIT) for s in range(SLOTS)]
    w_hi = [sb(f"w_hi{s}", [P, KU, N], F32R, ring + (2 * s + 1) * UNIT) for s in range(SLOTS)]
    ident = sb("ident", [P, P], F32, region(4 * P))
    bias_rows = sb("bias_rows", [P, G, P], F32, region(4 * G * P))
    final_g_rows = sb("final_g_rows", [P, D], F32, region(ROW))
    wsT = [sb(f"wsT_{n}", [P, G, P], F32R, region(4 * G * P)) for n in ("hi", "lo")]
    gains = sb("gains", [P, 3 * KD], F32, region(4 * 3 * KD))
    g_mix, g_mlp, g_v = (gains[:, i * KD:(i + 1) * KD] for i in range(3))
    ws_raw = sb("ws_raw", [P, G, P], F32, B)
    gain_rows = sb("gain_rows", [3 * KD, P], F32, B + 4 * G * P)
    relu_a = sb("relu_a", [P, TT, N], F32, region(TT * N * 4))
    biased = sb("biased", [P, 2, N], F32, region(2 * N * 4))
    junk = sb("junk", [P, D], BF16, region(2 * D))
    minus_half = sb("minus_half", [P, TT], F32, region(32))
    eps = sb("eps", [P, TT], F32, region(32))

    def stat(name):
        return sb(name, [P, TT], F32, region(32))

    x_sq, x_ms, x_rstd = stat("x_sq"), stat("x_ms"), stat("x_rstd")
    v_sq, v_ms, v_rstd = stat("v_sq"), stat("v_ms"), stat("v_rstd")
    x1_sq, x1_ms, x1_r2 = stat("x1_sq"), stat("x1_ms"), stat("x1_r2")
    o_sq, o_ms, o_rstd = stat("o_sq"), stat("o_ms"), stat("o_rstd")
    assert at[0] <= nc.sbuf_usable_end, (at[0], nc.sbuf_usable_end)

    def f32(ap):
        return ap.bitcast(F32)

    with ExitStack() as ctx:
        BANK = [[ctx.enter_context(nc.psum_tensor(f"bank{s}{j}", [P, N], F32)) for j in range(4)]
                for s in range(2)]

        def sem(name):
            return ctx.enter_context(nc.semaphore(name))

        w_loaded = [sem(f"w_loaded{s}") for s in range(SLOTS)]
        w_hi_done = sem("w_hi_done")
        w_ready = sem("w_ready")
        products = sem("products")
        mix_done = sem("mix_done")
        xT_done = sem("xT_done")
        x1T_done = sem("x1T_done")
        gains_loaded, ws_loaded = sem("gains_loaded"), sem("ws_loaded")
        bias_loaded, final_g_loaded = sem("bias_loaded"), sem("final_g_loaded")
        ident_zero, ident_done = sem("ident_zero"), sem("ident_done")
        half_done, ws_masked = sem("half_done"), sem("ws_masked")
        gains_T, gains_done = sem("gains_T"), sem("gains_done")
        ws_T, wsT_hi_done, wsT_done = sem("ws_T"), sem("wsT_hi_done"), sem("wsT_done")
        xin_loaded = [sem(f"xin_loaded{t}") for t in range(TT)]
        x1_loaded = sem("x1_loaded")
        squares = sem("squares")
        x_ms_done, x_rstd_done = sem("x_ms_done"), sem("x_rstd_done")
        xn_ready = sem("xn_ready")
        hT_hi_done, hT_ready = sem("hT_hi_done"), sem("hT_ready")
        v_gelu = sem("v_gelu")
        v_ms_done, v_rstd_done = sem("v_ms_done"), sem("v_rstd_done")
        v_hi_done, v_ready = sem("v_hi_done"), sem("v_ready")
        u_gelu = sem("u_gelu")
        mix_read, y_done = sem("mix_read"), sem("y_done")
        y_hi_done, y_ready = sem("y_hi_done"), sem("y_ready")
        x1_attn = sem("x1_attn")
        x1T_hi_done, x1T_ready = sem("x1T_hi_done"), sem("x1T_ready")
        x1_ms_done, x1_r2_done = sem("x1_ms_done"), sem("x1_r2_done")
        relu_done = sem("relu_done")
        a2_hi_done, a_squared, a2_ready = sem("a2_hi_done"), sem("a_squared"), sem("a2_ready")
        x1_mlp_done = sem("x1_mlp_done")
        o_ms_done, o_rstd_done = sem("o_ms_done"), sem("o_rstd_done")
        out_ready, stored = sem("out_ready"), sem("stored")

        def number(b, h):
            if isinstance(h, Turn):
                return b * UNITS + h.i * PER_TURN + h.h
            return b * UNITS + h

        def loaded_value(b, h):
            if isinstance(h, Turn):
                return b * (16 * UNITS // SLOTS) + h.i * (16 * PER_TURN // SLOTS) + 16 * (h.h // SLOTS + 1)
            return b * (16 * UNITS // SLOTS) + 16 * (h // SLOTS + 1)

        V_SQ, X1_SQ, X_SQ, O_SQ = 0, 1, 2, 3

        def squares_before(b, which):
            return b * (4 * TT) + (1 + which) * TT

        def bank_value(b, h, j):
            return number(b, h) * 4 + (j + 1)

        block = ctx.enter_context(nc.Block())

        @block.sync
        def _(sp):
            def load(b, h, src):
                if not (isinstance(b, int) and b == 0 and not isinstance(h, Turn) and h < SLOTS):
                    sp.wait_ge(products, bank_value(b, h - SLOTS, 3))
                return sp.dma_start(w_raw[slot_of(h)][:, :, :], src)

            def attention_unit(b, h):
                half = slice((h % 2) * KU, (h % 2 + 1) * KU)
                if h < UO:
                    c = (D if h < UU else 0) + (h // 2 % 2) * N
                    src = w_in_v[:, half, c:c + N]
                else:
                    c = (h - UO) // 2 * N
                    src = w_out_v[:, half, c:c + N]
                load(b, h, src).then_inc(w_loaded[h % SLOTS], 16)

            def m1_units(b, h, e):
                for a in range(2):
                    load(b, h + a, w1_v[e][:, a * KU:(a + 1) * KU, :])\
                        .then_inc(w_loaded[slot_of(h + a)], 16)

            def m2_units(b, h, e):
                for a in range(2):
                    load(b, h + a, w2_v[e][:, :, a * N:(a + 1) * N])\
                        .then_inc(w_loaded[slot_of(h + a)], 16)

            def block_loads(b, last):
                for h in range(SLOTS, UM):
                    attention_unit(b, h)
                m1_units(b, UM, 0)
                with sp.Fori(0, PAIRS) as i:
                    h = Turn(i, LOOP0)
                    m1_units(b, h, i * 2 + 1)
                    m2_units(b, h + 2, i * 2)
                    m1_units(b, h + 4, i * 2 + 2)
                    m2_units(b, h + 6, i * 2 + 1)
                m1_units(b, TAIL, GROUPS - 1)
                m2_units(b, TAIL + 2, GROUPS - 2)
                m2_units(b, TAIL + 4, GROUPS - 1)
                if not last:
                    sp.wait_ge(products, bank_value(b, TAIL + 1, 3))
                    input_tiles(b + 1)
                    for h in range(SLOTS):
                        attention_unit(b + 1, h)
                for t in range(TT):
                    sp.wait_ge(out_ready, b * TT + t + 1)
                    sp.dma_start(out_v[b][:, t, :], x1[:, t, :]).then_inc(stored, 16)
                if not last:
                    sp.wait_ge(stored, b * (16 * TT) + 16 * TT)
                    sp.dma_start(x1[:, :, :], x_v[b + 1]).then_inc(x1_loaded, 16)

            def input_tiles(q):
                for t in range(TT):
                    sp.dma_start(xin[:, t, :], x_v[q][:, t, :]).then_inc(xin_loaded[t], 16)

            input_tiles(0)
            attention_unit(0, 0)
            sp.dma_start(ws_raw[:, :, :], a_w_s.rearrange("a g t s -> t (a g) s")).then_inc(ws_loaded, 16)
            for h in range(1, SLOTS):
                attention_unit(0, h)
            sp.dma_start(bias_rows[:, :, :], a_b_s.partition_broadcast(P).rearrange("p a g t -> p (a g) t"))\
                .then_inc(bias_loaded, 16)
            sp.dma_start(final_g_rows[:, :], final_g.partition_broadcast(P)).then_inc(final_g_loaded, 16)
            sp.dma_start(x1[:, :, :], x_v[0]).then_inc(x1_loaded, 16)
            with sp.Fori(0, BLOCKS - 1) as b:
                block_loads(b, False)
            block_loads(BLOCKS - 1, True)
            sp.wait_ge(stored, 16 * TT * BLOCKS)

        @block.gpsimd
        def _(pool):
            pool.memset(ident[:, :], 0.0).then_inc(ident_zero, 1)
            pool.wait_ge(ident_zero, 1)
            pool.affine_select(out=ident[:, :], in_=ident[:, :], compare_op=ALU.not_equal, fill=1.0,
                               base=0, pattern=[[-1, P]], channel_multiplier=1).then_inc(ident_done, 1)
            pool.memset(minus_half[:, :], -0.5).then_inc(half_done, 1)
            pool.memset(eps[:, :], EPS).then_inc(half_done, 1)
            pool.wait_ge(half_done, 2)

            def rstd(sq, before, ms, ms_done, r, r_done, n):
                for t in range(TT):
                    pool.wait_ge(squares, before + (t + 1))
                    pool.tensor_tensor(ms[:, t:t + 1], sq[:, t:t + 1], eps[:, t:t + 1], ALU.add)\
                        .then_inc(ms_done, 1)
                    pool.wait_ge(ms_done, n * TT + (t + 1))
                    pool.tensor_tensor(r[:, t:t + 1], ms[:, t:t + 1], minus_half[:, t:t + 1], ALU.pow)\
                        .then_inc(r_done, 1)

            def block_norms(b, last):
                rstd(v_sq, squares_before(b, V_SQ), v_ms, v_ms_done, v_rstd, v_rstd_done, b)
                if not last:
                    rstd(x_sq, squares_before(b, X_SQ), x_ms, x_ms_done, x_rstd, x_rstd_done, b + 1)
                rstd(o_sq, squares_before(b, X_SQ if last else O_SQ), o_ms, o_ms_done, o_rstd, o_rstd_done, b)

            rstd(x_sq, 0, x_ms, x_ms_done, x_rstd, x_rstd_done, 0)
            pool.wait_ge(ws_loaded, 16)
            pool.affine_select(out=ws_raw[:, :, :], in_=ws_raw[:, :, :], compare_op=ALU.is_ge, fill=0.0,
                               base=0, pattern=[[0, G], [-1, P]], channel_multiplier=1)\
                .then_inc(ws_masked, 1)
            with pool.Fori(0, BLOCKS - 1) as b:
                block_norms(b, False)
            block_norms(BLOCKS - 1, True)

        @block.scalar
        def _(act):
            def split_hi(b, h):
                act.wait_ge(w_loaded[slot_of(h)], loaded_value(b, h))
                act.activation(w_hi[slot_of(h)][:, :, :], w_raw[slot_of(h)][:, :, :], ACT.Copy)\
                    .then_inc(w_hi_done, 1)

            def gelu_v(b, half):
                for t in range(TT):
                    act.wait_ge(products, bank_value(b, UV + 2 * half + 1, t))
                    act.activation(vf[:, t, half * N:(half + 1) * N], BANK[half][t][:, :],
                                   ACT.Gelu_apprx_tanh).then_inc(v_gelu, 1)

            def gelu_u(b, half):
                for j in range(4):
                    act.wait_ge(products, bank_value(b, UU + 2 * half + 1, j))
                    act.activation(uT[:, 4 * half + j, :], BANK[half][j][:, :],
                                   ACT.Gelu_apprx_tanh).then_inc(u_gelu, 1)

            def mean_squares(rows, sq, start, ready=None):
                for t in range(TT):
                    if ready:
                        ready(t)
                    if not (isinstance(start, int) and start + t == 0):
                        act.wait_ge(squares, start + t)
                    act.activation(junk[:, :], rows[:, t, :], ACT.Square, scale=D ** -0.5,
                                   accum_out=sq[:, t:t + 1]).then_inc(squares, 1)

            def split_v(b):
                for t in range(TT):
                    act.wait_ge(v_rstd_done, b * TT + (t + 1))
                    act.activation(vn[HI][:, t, :], vf[:, t, :], ACT.Copy, scale=v_rstd[:, t:t + 1])\
                        .then_inc(v_hi_done, 1)

            def split_y(b, g):
                act.wait_ge(y_done, b * G + g + 1)
                act.activation(yT[HI][:, g, :], uT[:, g, :], ACT.Copy).then_inc(y_hi_done, 1)

            def split_transposed(q, half, done, dst, gain, hi_done, s):
                for j in range(4):
                    k = 4 * half + j
                    act.wait_ge(done, q * KD + k + 1)
                    act.activation(dst[HI][:, k, :], BANK[s][j][:, :], ACT.Copy,
                                   scale=gain[:, k:k + 1]).then_inc(hi_done, 1)

            def relu_squared(b, h, e, parity, s, first=False):
                for j in range(4):
                    act.wait_ge(products, bank_value(b, h + 1, j))
                    if not first:
                        act.wait_ge(a2_ready, b * M1S + (e - 1) * TT + j + 1)
                    act.activation(relu_a[:, j, :], BANK[s][j][:, :], ACT.Relu).then_inc(relu_done, 1)
                for j in range(4):
                    act.wait_ge(relu_done, b * M1S + e * TT + j + 1)
                    act.activation(a2[parity][HI][:, j, :], relu_a[:, j, :], ACT.Square)\
                        .then_inc(a2_hi_done, 1)

            def block_act(b, last):
                split_hi(b, 2)
                split_hi(b, 3)
                gelu_v(b, 0)
                split_hi(b, 4)
                split_hi(b, 5)
                gelu_v(b, 1)
                act.wait_ge(v_gelu, b * (2 * TT) + 2 * TT)
                mean_squares(vf, v_sq, squares_before(b, V_SQ))
                split_hi(b, 6)
                split_v(b)
                split_hi(b, 7)
                gelu_u(b, 0)
                split_hi(b, 8)
                split_hi(b, 9)
                gelu_u(b, 1)
                for g in range(G):
                    split_y(b, g)
                    if g == 3:
                        split_hi(b, 10)
                split_hi(b, 11)
                split_transposed(b, 0, x1T_done, x1T, g_mlp, x1T_hi_done, 0)
                split_hi(b, 12)
                split_hi(b, 13)
                split_transposed(b, 1, x1T_done, x1T, g_mlp, x1T_hi_done, 1)
                split_hi(b, 14)
                act.wait_ge(x1_attn, b * (2 * TT) + 2 * TT)
                mean_squares(x1, x1_sq, squares_before(b, X1_SQ))
                split_hi(b, 15)
                relu_squared(b, UM, 0, 0, 0, first=True)
                with act.Fori(0, PAIRS) as i:
                    h = Turn(i, LOOP0)
                    split_hi(b, h + 2)
                    split_hi(b, h + 3)
                    relu_squared(b, h, i * 2 + 1, 1, 1)
                    split_hi(b, h + 4)
                    split_hi(b, h + 5)
                    split_hi(b, h + 6)
                    split_hi(b, h + 7)
                    relu_squared(b, h + 4, i * 2 + 2, 0, 0)
                    split_hi(b, h + 8)
                    split_hi(b, h + 9)
                split_hi(b, TAIL + 2)
                split_hi(b, TAIL + 3)
                relu_squared(b, TAIL, GROUPS - 1, 1, 1)
                split_hi(b, TAIL + 4)
                if not last:
                    mean_squares(xin, x_sq, squares_before(b, X_SQ),
                                 lambda t: act.wait_ge(xin_loaded[t], b * 16 + 32))
                split_hi(b, TAIL + 5)
                if not last:
                    split_hi(b + 1, 0)
                    split_transposed(b + 1, 0, xT_done, hT, g_mix, hT_hi_done, 1)
                    split_hi(b + 1, 1)
                    split_transposed(b + 1, 1, xT_done, hT, g_mix, hT_hi_done, 0)
                mean_squares(x1, o_sq, squares_before(b, X_SQ if last else O_SQ),
                             lambda t: act.wait_ge(x1_mlp_done, b * M2S + (M2S - TT + t + 1 + PRIMED)))

            for i, g in enumerate((norm_mix_g, norm_mlp_g, a_v_g)):
                act.dma_start(gain_rows[i * KD:(i + 1) * KD, :],
                              g.rearrange("a (k p) -> (a k) p", p=P)).then_inc(gains_loaded, 16)
            mean_squares(xin, x_sq, 0, lambda t: act.wait_ge(xin_loaded[t], 16))
            split_transposed(0, 0, xT_done, hT, g_mix, hT_hi_done, 1)
            split_hi(0, 0)
            split_transposed(0, 1, xT_done, hT, g_mix, hT_hi_done, 0)
            split_hi(0, 1)
            for s in range(2):
                act.wait_ge(ws_T, 4 * s + 4)
                act.activation(wsT[HI][:, 4 * s:4 * s + 4, :], BANK[1][s][:, :], ACT.Copy)\
                    .then_inc(wsT_hi_done, 1)
            with act.Fori(0, BLOCKS - 1) as b:
                block_act(b, False)
            block_act(BLOCKS - 1, True)

        @block.vector
        def _(dve):
            def split_lo(b, h):
                dve.wait_ge(w_hi_done, number(b, h) + 1)
                dve.tensor_tensor(w_lo[slot_of(h)][:, :, :], w_raw[slot_of(h)][:, :, :],
                                  f32(w_hi[slot_of(h)][:, :, :]), ALU.subtract).then_inc(w_ready, 1)

            def split_transposed(q, half, dst, gain, hi_done, ready, s):
                for j in range(4):
                    k = 4 * half + j
                    dve.wait_ge(hi_done, q * KD + k + 1)
                    dve.scalar_tensor_tensor(out=dst[LO][:, k, :], in0=BANK[s][j][:, :],
                                             scalar=gain[:, k:k + 1], in1=f32(dst[HI][:, k, :]),
                                             op0=ALU.mult, op1=ALU.subtract).then_inc(ready, 1)

            def norm_input(q):
                for t in range(TT):
                    dve.wait_ge(x_rstd_done, q * TT + (t + 1))
                    dve.tensor_scalar(xin[:, t, :], xin[:, t, :], x_rstd[:, t:t + 1], None, ALU.mult)\
                        .then_inc(xn_ready, 1)

            def split_v(b):
                for t in range(TT):
                    dve.wait_ge(v_hi_done, b * TT + t + 1)
                    dve.scalar_tensor_tensor(out=vn[LO][:, t, :], in0=vf[:, t, :],
                                             scalar=v_rstd[:, t:t + 1], in1=f32(vn[HI][:, t, :]),
                                             op0=ALU.mult, op1=ALU.subtract).then_inc(v_ready, 1)

            def gate(b, g):
                dve.wait_ge(mix_done, b * G + g + 1)
                dve.scalar_tensor_tensor(
                    out=biased[:, g % 2, :].rearrange("p (n t) -> p n t", t=P),
                    in0=BANK[g // 4][g % 4][:, :].rearrange("p (n t) -> p n t", t=P),
                    scalar=g_v[:, g:g + 1], in1=bias_rows[:, g:g + 1, :].to_broadcast([P, TT, P]),
                    op0=ALU.mult, op1=ALU.add).then_inc(mix_read, 1)
                dve.wait_ge(mix_read, b * G + g + 1)
                dve.tensor_tensor(uT[:, g, :], uT[:, g, :], biased[:, g % 2, :], ALU.mult)\
                    .then_inc(y_done, 1)

            def split_y(b, g):
                dve.wait_ge(y_hi_done, b * G + g + 1)
                dve.tensor_tensor(yT[LO][:, g, :], uT[:, g, :], f32(yT[HI][:, g, :]), ALU.subtract)\
                    .then_inc(y_ready, 1)

            def add_attention(b, half):
                for t in range(TT):
                    dve.wait_ge(products, bank_value(b, UO + 2 * half + 1, t))
                    rows = x1[:, t, half * N:(half + 1) * N]
                    dve.tensor_tensor(rows, BANK[half][t][:, :], rows, ALU.add).then_inc(x1_attn, 1)

            def relu_squared(b, e, parity):
                for j in range(4):
                    dve.wait_ge(a2_hi_done, b * M1S + e * TT + j + 1)
                    dve.tensor_tensor(relu_a[:, j, :], relu_a[:, j, :], relu_a[:, j, :], ALU.mult)\
                        .then_inc(a_squared, 1)
                for j in range(4):
                    dve.wait_ge(a_squared, b * M1S + e * TT + j + 1)
                    dve.tensor_tensor(a2[parity][LO][:, j, :], relu_a[:, j, :],
                                      f32(a2[parity][HI][:, j, :]), ALU.subtract).then_inc(a2_ready, 1)

            def add_mlp(b, h, half, s, tiles=range(TT)):
                for t in tiles:
                    dve.wait_ge(products, bank_value(b, h, t))
                    rows = x1[:, t, half * N:(half + 1) * N]
                    dve.scalar_tensor_tensor(out=rows, in0=BANK[s][t][:, :], scalar=x1_r2[:, t:t + 1],
                                             in1=rows, op0=ALU.mult, op1=ALU.add)\
                        .then_inc(x1_mlp_done, 1)

            def scale_out(b, t):
                dve.wait_ge(o_rstd_done, b * TT + (t + 1))
                dve.scalar_tensor_tensor(out=x1[:, t, :], in0=x1[:, t, :], scalar=o_rstd[:, t:t + 1],
                                         in1=final_g_rows[:, :], op0=ALU.mult, op1=ALU.mult)\
                    .then_inc(out_ready, 1)

            def block_dve(b, last):
                for h in (2, 3, 4, 5, 6):
                    split_lo(b, h)
                split_v(b)
                for h in (7, 8, 9):
                    split_lo(b, h)
                for g in range(G + 1):
                    if g < G:
                        if g == 0:
                            dve.wait_ge(u_gelu, b * G + 4)
                        if g >= 4:
                            dve.wait_ge(u_gelu, b * G + g + 1)
                        gate(b, g)
                    if g >= 1:
                        split_y(b, g - 1)
                    if g == 4:
                        split_lo(b, 10)
                split_lo(b, 11)
                dve.wait_ge(x1_loaded, b * 16 + 16)
                add_attention(b, 0)
                split_transposed(b, 0, x1T, g_mlp, x1T_hi_done, x1T_ready, 0)
                split_lo(b, 12)
                split_lo(b, 13)
                add_attention(b, 1)
                split_transposed(b, 1, x1T, g_mlp, x1T_hi_done, x1T_ready, 1)
                split_lo(b, 14)
                dve.wait_ge(squares, squares_before(b, X1_SQ) + TT)
                dve.tensor_scalar(x1_ms[:, :], x1_sq[:, :], EPS, None, ALU.add)\
                    .then_inc(x1_ms_done, 1)
                dve.wait_ge(x1_ms_done, b + 1)
                dve.reciprocal(x1_r2[:, :], x1_ms[:, :]).then_inc(x1_r2_done, 1)
                dve.wait_ge(x1_r2_done, b + 1)
                split_lo(b, 15)
                relu_squared(b, 0, 0)
                with dve.Fori(0, PAIRS) as i:
                    h = Turn(i, LOOP0)
                    split_lo(b, h + 2)
                    split_lo(b, h + 3)
                    relu_squared(b, i * 2 + 1, 1)
                    split_lo(b, h + 4)
                    add_mlp(b, h + 2, 0, 0)
                    split_lo(b, h + 5)
                    add_mlp(b, h + 3, 1, 1)
                    split_lo(b, h + 6)
                    split_lo(b, h + 7)
                    relu_squared(b, i * 2 + 2, 0)
                    split_lo(b, h + 8)
                    add_mlp(b, h + 6, 0, 1)
                    split_lo(b, h + 9)
                    add_mlp(b, h + 7, 1, 0)
                split_lo(b, TAIL + 2)
                split_lo(b, TAIL + 3)
                relu_squared(b, GROUPS - 1, 1)
                split_lo(b, TAIL + 4)
                add_mlp(b, TAIL + 2, 0, 0)
                if not last:
                    norm_input(b + 1)
                split_lo(b, TAIL + 5)
                add_mlp(b, TAIL + 3, 1, 1)
                if not last:
                    split_lo(b + 1, 0)
                    split_transposed(b + 1, 0, hT, g_mix, hT_hi_done, hT_ready, 1)
                add_mlp(b, TAIL + 4, 0, 0)
                if not last:
                    split_lo(b + 1, 1)
                    split_transposed(b + 1, 1, hT, g_mix, hT_hi_done, hT_ready, 0)
                for t in range(TT + 1):
                    if t < TT:
                        add_mlp(b, TAIL + 5, 1, 1, (t,))
                    if t >= 1:
                        scale_out(b, t - 1)

            dve.sem_inc(x1_mlp_done, PRIMED)
            dve.wait_ge(gains_T, 1)
            dve.tensor_copy(gains[:, :], BANK[0][0][:, 0:3 * KD]).then_inc(gains_done, 1)
            norm_input(0)
            dve.wait_ge(gains_done, 1)
            split_transposed(0, 0, hT, g_mix, hT_hi_done, hT_ready, 1)
            split_lo(0, 0)
            split_transposed(0, 1, hT, g_mix, hT_hi_done, hT_ready, 0)
            split_lo(0, 1)
            for s in range(2):
                dve.wait_ge(wsT_hi_done, s + 1)
                dve.tensor_tensor(wsT[LO][:, 4 * s:4 * s + 4, :],
                                  BANK[1][s][:, :].rearrange("p (g t) -> p g t", t=P),
                                  f32(wsT[HI][:, 4 * s:4 * s + 4, :]), ALU.subtract).then_inc(wsT_done, 1)
            dve.wait_ge(bias_loaded, 16)
            dve.wait_ge(final_g_loaded, 16)
            with dve.Fori(0, BLOCKS - 1) as b:
                block_dve(b, False)
            block_dve(BLOCKS - 1, True)

        @block.tensor
        def _(pe):
            def unit(b, h, s, first, final, stationary, moving, between=None, by_bank=False):
                pe.wait_ge(w_ready, number(b, h) + 1)
                steps = [(k, j) for k in range(KU) for j in range(4)]
                if by_bank:
                    steps = [(k, j) for j in range(4) for k in range(KU)]
                for step, (k, j) in enumerate(steps):
                    if step == len(steps) // 2 and between:
                        between()
                    for n, (x_part, y_part) in enumerate(PASSES):
                        ins = pe.matmul(BANK[s][j][:, :], stationary(x_part, k, j),
                                        moving(y_part, k, j), start=first and k == 0 and n == 0,
                                        stop=final and k == KU - 1 and n == 2)
                    if final and k == KU - 1:
                        ins.then_inc(products, 1)
                if not final:
                    ins.then_inc(products, 4)

            def token_major(operand, b, h, s, first, final, k0=0, between=None, by_bank=False):
                unit(b, h, s, first, final,
                     lambda part, k, j: operand[part][:, k0 + k, j * P:(j + 1) * P],
                     lambda part, k, j: (w_hi, w_lo)[part][slot_of(h)][:, k, :], between, by_bank)

            def feature_major(operand, b, h, s, first, final, k0=0, between=None):
                unit(b, h, s, first, final,
                     lambda part, k, j: (w_hi, w_lo)[part][slot_of(h)][:, k, j * P:(j + 1) * P],
                     lambda part, k, j: operand[part][:, k0 + k, :], between)

            def transposes(rows, half, s, done, ready=None):
                for t in range(TT):
                    if ready:
                        ready(t)
                    for j in range(4):
                        k = 4 * half + j
                        ins = pe.transpose(BANK[s][j][:, t * P:(t + 1) * P],
                                           rows[:, t, k * P:(k + 1) * P], ident[:, :])
                        if t == TT - 1:
                            ins.then_inc(done, 1)

            def mix(b):
                pe.wait_ge(v_ready, b * TT + TT)
                pe.wait_ge(u_gelu, b * G + 4)
                for g in range(G):
                    if g >= 4:
                        pe.wait_ge(u_gelu, b * G + g + 1)
                    for t in range(TT):
                        for n, (x_part, y_part) in enumerate(PASSES):
                            ins = pe.matmul(BANK[g // 4][g % 4][:, t * P:(t + 1) * P],
                                            vn[x_part][:, t, g * P:(g + 1) * P],
                                            wsT[y_part][:, g, :], start=n == 0, stop=n == 2)
                    ins.then_inc(mix_done, 1)

            def group_up(b, h, s):
                for a in range(2):
                    feature_major(x1T, b, h + a, s, a == 0, a == 1, a * KU)

            def mlp_added(b, banks):
                pe.wait_ge(x1_mlp_done, b * M2S + banks + PRIMED)

            def block_pe(b, last):
                pe.wait_ge(hT_ready, b * KD + KD)
                for half in range(2):
                    if half == 1:
                        pe.wait_ge(wsT_done, 2)
                    for a in range(2):
                        token_major(hT, b, UV + 2 * half + a, half, a == 0, a == 1, a * KU)
                for half in range(2):
                    pe.wait_ge(v_gelu, b * (2 * TT) + TT * (half + 1))
                    for a in range(2):
                        feature_major(hT, b, UU + 2 * half + a, half, a == 0, a == 1, a * KU)
                mix(b)
                pe.wait_ge(mix_read, b * G + 4)
                for a in range(2):
                    pe.wait_ge(w_ready, number(b, UO + a) + 1)
                    for k in range(KU):
                        g = a * KU + k
                        pe.wait_ge(y_ready, b * G + g + 1)
                        for j in range(4):
                            for n, (x_part, y_part) in enumerate(PASSES):
                                ins = pe.matmul(BANK[0][j][:, :], yT[x_part][:, g, j * P:(j + 1) * P],
                                                (w_hi, w_lo)[y_part][(UO + a) % SLOTS][:, k, :],
                                                start=g == 0 and n == 0, stop=g == G - 1 and n == 2)
                            if g == G - 1:
                                ins.then_inc(products, 1)
                    if a == 0:
                        ins.then_inc(products, 4)

                def x1_half(half):
                    pe.wait_ge(x1_attn, b * (2 * TT) + TT * (half + 1))
                    transposes(x1, half, half, x1T_done)

                token_major(yT, b, UO + 2, 1, True, False, 0, between=lambda: x1_half(0))
                token_major(yT, b, UO + 3, 1, False, True, KU)
                pe.wait_ge(x1T_ready, b * KD + 4)
                feature_major(x1T, b, UM, 0, True, False, 0, between=lambda: x1_half(1))
                pe.wait_ge(x1T_ready, b * KD + 8)
                feature_major(x1T, b, UM + 1, 0, False, True, KU)
                with pe.Fori(0, PAIRS) as i:
                    h = Turn(i, LOOP0)
                    mlp_added(b, i * 16 - 4)
                    group_up(b, h, 1)
                    pe.wait_ge(a2_ready, b * M1S + i * 8 + 4)
                    mlp_added(b, i * 16)
                    token_major(a2[0], b, h + 2, 0, True, True)
                    pe.wait_ge(relu_done, b * M1S + i * 8 + 8)
                    token_major(a2[0], b, h + 3, 1, True, True)
                    mlp_added(b, i * 16 + 4)
                    group_up(b, h + 4, 0)
                    pe.wait_ge(a2_ready, b * M1S + i * 8 + 8)
                    mlp_added(b, i * 16 + 8)
                    token_major(a2[1], b, h + 6, 1, True, True)
                    pe.wait_ge(relu_done, b * M1S + i * 8 + 12)
                    token_major(a2[1], b, h + 7, 0, True, True)
                E = GROUPS
                mlp_added(b, 8 * (E - 3) + 4)
                group_up(b, TAIL, 1)
                pe.wait_ge(a2_ready, b * M1S + 4 * (E - 1))
                mlp_added(b, 8 * (E - 2))
                token_major(a2[0], b, TAIL + 2, 0, True, True)
                pe.wait_ge(relu_done, b * M1S + 4 * E)
                token_major(a2[0], b, TAIL + 3, 1, True, True)

                def x_half(half, banks):
                    mlp_added(b, banks)
                    transposes(xin, half, 1 - half, xT_done,
                               lambda t: pe.wait_ge(xn_ready, b * TT + (TT + t + 1)))

                pe.wait_ge(a2_ready, b * M1S + 4 * E)
                mlp_added(b, 8 * (E - 2) + 4)
                token_major(a2[1], b, TAIL + 4, 0, True, True,
                            between=None if last else lambda: x_half(0, 8 * (E - 1)))
                if last:
                    mlp_added(b, 8 * (E - 1))
                else:
                    pe.wait_ge(hT_ready, b * KD + KD + 4)
                token_major(a2[1], b, TAIL + 5, 1, True, True,
                            between=None if last else lambda: x_half(1, 8 * (E - 1) + 4), by_bank=True)

            pe.wait_ge(ident_done, 1)
            pe.wait_ge(gains_loaded, 3 * 16)
            pe.transpose(BANK[0][0][:, 0:3 * KD], gain_rows[:, :], ident[0:3 * KD, 0:3 * KD])\
                .then_inc(gains_T, 1)
            transposes(xin, 0, 1, xT_done, lambda t: pe.wait_ge(xn_ready, t + 1))
            pe.wait_ge(gains_done, 1)
            transposes(xin, 1, 0, xT_done)
            pe.wait_ge(hT_ready, 4)
            pe.wait_ge(ws_masked, 1)
            for g in range(G):
                pe.transpose(BANK[1][g // 4][:, g % 4 * P:(g % 4 + 1) * P], ws_raw[:, g, :], ident[:, :])\
                    .then_inc(ws_T, 1)
            with pe.Fori(0, BLOCKS - 1) as b:
                block_pe(b, False)
            block_pe(BLOCKS - 1, True)


_INS = ["x", "norm_mix_g", "norm_mlp_g", "final_g", "a_w_in", "a_v_g", "a_w_s", "a_b_s", "a_w_out",
        "mlp_w1", "mlp_w2"]


def kernel(**inputs):
    import numpy as np
    import concourse.bacc as bacc
    from concourse.bass_utils import run_bass_kernel_spmd

    nc = bacc.Bacc("TRN2", target_bir_lowering=False, num_devices=1)
    arrays, args = {}, []
    for name in _INS:
        a = np.ascontiguousarray(inputs[name])
        arrays[f"in_{name}"] = a
        args.append(nc.dram_tensor(f"in_{name}", a.shape, mybir.dt.from_np(a.dtype),
                                   kind="ExternalInput").ap())
    out = nc.dram_tensor("out", inputs["x"].shape, F32, kind="ExternalOutput").ap()
    build(nc, *args, out)
    result = run_bass_kernel_spmd(nc, [arrays], core_ids=[0])
    return result.results[0]["out"]
```
